# Optimizing a Trainium2 kernel written in Bass

```python
import math
import jax, jax.numpy as jnp
from jax import lax
import numpy as np

D_MODEL = 2048
BATCH = 1
SEQ = 128
DEPTH = 1
DEC_BATCH = 1
DEC_SEQ = 256
PAST_LEN = 128

GRID_W = 64
HEAD_DIM = 128
Q_BLOCK = 128
EPS = 1e-6
ROPE_THETA = 10000.0
DA_HEADS = 4
DA_DH = HEAD_DIM // 2
LRU_WIDTH = 512
LRU_BLOCKS = 4
LRU_BS = LRU_WIDTH // LRU_BLOCKS
LRU_C = 8.0
CONV_W = 4
CONV_LEFT = 2
NA_HEADS = 4
NA_ROWS = 8
NA_COLS = 16
GQA_Q_HEADS = 4
GQA_KV_HEADS = 2
IN_SPLITS = (DA_HEADS * HEAD_DIM, DA_HEADS * HEAD_DIM, DA_HEADS * HEAD_DIM,
             LRU_WIDTH, LRU_WIDTH,
             NA_HEADS * HEAD_DIM, NA_HEADS * HEAD_DIM, NA_HEADS * HEAD_DIM,
             GQA_Q_HEADS * HEAD_DIM, GQA_KV_HEADS * HEAD_DIM, GQA_KV_HEADS * HEAD_DIM)
IN_WIDTH = sum(IN_SPLITS)
MIX_WIDTH = DA_HEADS * HEAD_DIM + LRU_WIDTH + NA_HEADS * HEAD_DIM + GQA_Q_HEADS * HEAD_DIM
FFN_HIDDEN = ((8 * D_MODEL // 3 + 255) // 256) * 256

kernel_name = "hybrid_diffusion_parallel_heads_step"

def rmsnorm(x, g=None):
    xf = x.astype(jnp.float32)
    y = xf * lax.rsqrt(jnp.mean(xf * xf, axis=-1, keepdims=True) + EPS)
    if g is not None:
        y = y * g.astype(jnp.float32)
    return y.astype(x.dtype)

def axial_rope(x):
    n = x.shape[1]
    m = x.shape[-1] // 2
    t = jnp.arange(n)
    freqs = ROPE_THETA ** (-jnp.arange(0, m, 2, dtype=jnp.float32) / m)
    bshape = (n,) + (1,) * (x.ndim - 3) + (m // 2,)

    def rot(xh, pos):
        ang = (pos.astype(jnp.float32)[:, None] * freqs).reshape(bshape)
        cos = jnp.cos(ang).astype(x.dtype)
        sin = jnp.sin(ang).astype(x.dtype)
        x1, x2 = jnp.split(xh, 2, axis=-1)
        return jnp.concatenate([x1 * cos - x2 * sin, x1 * sin + x2 * cos], axis=-1)

    return jnp.concatenate([rot(x[..., :m], t // GRID_W), rot(x[..., m:], t % GRID_W)], axis=-1)

def sweep_query_blocks(fn, q):
    b, sq = q.shape[:2]
    nb = sq // Q_BLOCK
    qb = jnp.moveaxis(q.reshape((b, nb, Q_BLOCK) + q.shape[2:]), 1, 0)
    out = jnp.moveaxis(lax.map(fn, qb), 0, 1)
    return out.reshape((b, sq) + out.shape[3:])

def diff_attention(q, k, v, lam, lam_init):
    scale = DA_DH ** -0.5

    def block(qb):
        s = jnp.einsum('bqhcd,bkhcd->bhcqk', qb, k).astype(jnp.float32) * scale
        p = jax.nn.softmax(s, axis=-1)
        p = p[:, :, 0] - lam * p[:, :, 1]
        return jnp.einsum('bhqk,bkhd->bqhd', p.astype(v.dtype), v)

    o = sweep_query_blocks(block, q)
    return rmsnorm(o) * (1.0 - lam_init)

def gqa_attention(q, k, v):
    b, sq, hq, d = q.shape
    hkv = k.shape[2]
    qg = q.reshape(b, sq, hkv, hq // hkv, d)
    scale = d ** -0.5

    def block(qb):
        s = jnp.einsum('bqngd,bsnd->bngqs', qb, k).astype(jnp.float32) * scale
        p = jax.nn.softmax(s, axis=-1).astype(v.dtype)
        return jnp.einsum('bngqs,bsnd->bqngd', p, v)

    return sweep_query_blocks(block, qg).reshape(b, sq, hq, d)

def neighbourhood_attention(q, k, v, k_ctx, v_ctx, rpb):
    b, n, h, d = q.shape
    rows = n // GRID_W
    kr = min(NA_ROWS, rows)
    scale = d ** -0.5
    qg = q.reshape(b, rows, GRID_W, h, d)
    kg = k.reshape(b, rows, GRID_W, h, d)
    vg = v.reshape(b, rows, GRID_W, h, d)
    w_idx = np.arange(GRID_W)
    col_start = np.clip(w_idx - NA_COLS // 2, 0, GRID_W - NA_COLS)
    col_idx = col_start[:, None] + np.arange(NA_COLS)[None, :]
    rpb_cols = rpb[:, :, col_idx - w_idx[:, None] + NA_COLS - 1]
    n_loc = kr * NA_COLS

    def row_block(args):
        r, qr = args
        start = jnp.clip(r - kr // 2, 0, rows - kr)
        kw = lax.dynamic_slice_in_dim(kg, start, kr, axis=1)[:, :, col_idx]
        vw = lax.dynamic_slice_in_dim(vg, start, kr, axis=1)[:, :, col_idx]
        s_loc = jnp.einsum('bwhd,biwjhd->bhwij', qr, kw).astype(jnp.float32) * scale
        row_off = start + jnp.arange(kr) - r + NA_ROWS - 1
        bias = jnp.transpose(rpb_cols[:, row_off], (0, 2, 1, 3)).astype(jnp.float32)
        s_loc = (s_loc + bias[None]).reshape(b, h, GRID_W, n_loc)
        s_ctx = jnp.einsum('bwhd,bphd->bhwp', qr, k_ctx).astype(jnp.float32) * scale
        p = jax.nn.softmax(jnp.concatenate([s_loc, s_ctx], axis=-1), axis=-1).astype(v.dtype)
        p_loc = p[..., :n_loc].reshape(b, h, GRID_W, kr, NA_COLS)
        return (jnp.einsum('bhwij,biwjhd->bwhd', p_loc, vw)
                + jnp.einsum('bhwp,bphd->bwhd', p[..., n_loc:], v_ctx))

    o = lax.map(row_block, (jnp.arange(rows), jnp.moveaxis(qg, 1, 0)))
    return jnp.moveaxis(o, 0, 1).reshape(b, n, h, d)

def centred_conv(x, w, bias):
    s = x.shape[1]
    xp = jnp.pad(x, ((0, 0), (CONV_LEFT, CONV_W - 1 - CONV_LEFT), (0, 0)))
    return bias + sum(xp[:, j:j + s] * w[j] for j in range(CONV_W))

def rglru_coeffs(x, gate_w, gate_b, lam_param):
    b, s, c = x.shape
    xb = x.reshape(b, s, LRU_BLOCKS, LRU_BS)
    gates = jnp.einsum('bsnc,gncd->gbsnd', xb, gate_w).reshape(2, b, s, c) + gate_b[:, None, None, :]
    r, i = jax.nn.sigmoid(gates.astype(jnp.float32))
    log_a = -LRU_C * r * jax.nn.softplus(-lam_param.astype(jnp.float32))
    a = jnp.exp(log_a)
    mult = jnp.sqrt(-jnp.expm1(2.0 * log_a))
    return a, mult * i * x.astype(jnp.float32)

def linear_scan(a, bx, h0, reverse):
    if reverse:
        a, bx = jnp.flip(a, 1), jnp.flip(bx, 1)
    bx = bx.at[:, 0].add(a[:, 0] * h0)

    def combine(e1, e2):
        a1, b1 = e1
        a2, b2 = e2
        return a1 * a2, a2 * b1 + b2

    _, h = lax.associative_scan(combine, (a, bx), axis=1)
    final = h[:, -1]
    if reverse:
        h = jnp.flip(h, 1)
    return h, final

def rglru_bidir(xb, gb, conv_w, conv_b, gate_w, gate_b, lam_param, h0):
    xc = centred_conv(xb, conv_w, conv_b)
    a_f, b_f = rglru_coeffs(xc, gate_w[0], gate_b[0], lam_param[0])
    h_f, fin_f = linear_scan(a_f, b_f, h0[:, 0].astype(jnp.float32), False)
    a_b, b_b = rglru_coeffs(xc, gate_w[1], gate_b[1], lam_param[1])
    h_b, fin_b = linear_scan(a_b, b_b, h0[:, 1].astype(jnp.float32), True)
    y = (h_f + h_b).astype(xb.dtype) * jax.nn.gelu(gb)
    return y, jnp.stack([fin_f, fin_b], axis=1).astype(xb.dtype)

def split_in(u):
    return jnp.split(u, np.cumsum(IN_SPLITS)[:-1].tolist(), axis=-1)

def setup_inputs(seed: int = 0) -> dict:
    key = jax.random.key(seed)
    ks = jax.random.split(key, 24)

    def nrm(k, shape, scale):
        return scale * jax.random.normal(k, shape, jnp.float32)

    u = jax.random.uniform(ks[17], (DEPTH, 2, LRU_WIDTH), jnp.float32, 0.9, 0.999)
    s = u ** (1.0 / LRU_C)
    lru_lambda = jnp.log(s) - jnp.log1p(-s)
    return {
        "x_prompt": nrm(ks[0], (BATCH, SEQ, D_MODEL), 1.0),
        "x_sample": nrm(ks[1], (DEC_BATCH, DEC_SEQ, D_MODEL), 1.0),
        "cache_diff_kv": nrm(ks[2], (DEC_BATCH, DEPTH, 2, PAST_LEN, DA_HEADS, HEAD_DIM), 1.0),
        "state_rglru": nrm(ks[3], (DEC_BATCH, DEPTH, 2, LRU_WIDTH), 0.5),
        "cache_na_kv": nrm(ks[4], (DEC_BATCH, DEPTH, 2, PAST_LEN, NA_HEADS, HEAD_DIM), 1.0),
        "cache_gqa_kv": nrm(ks[5], (DEC_BATCH, DEPTH, 2, PAST_LEN, GQA_KV_HEADS, HEAD_DIM), 1.0),
        "c": nrm(ks[6], (DEC_BATCH, D_MODEL), 1.0),
        "c_ctx": nrm(ks[7], (D_MODEL,), 1.0),
        "w_mod": nrm(ks[8], (DEPTH, D_MODEL, 6 * D_MODEL), 0.5 * D_MODEL ** -0.5),
        "b_mod": nrm(ks[9], (DEPTH, 6 * D_MODEL), 0.01),
        "norm_g": 1.0 + nrm(ks[10], (DEPTH, 4, D_MODEL), 0.05),
        "w_in": nrm(ks[11], (DEPTH, D_MODEL, IN_WIDTH), D_MODEL ** -0.5),
        "diff_lambda_w": nrm(ks[12], (DEPTH, 4, DA_DH), 0.1),
        "lru_conv_w": nrm(ks[13], (DEPTH, CONV_W, LRU_WIDTH), CONV_W ** -0.5),
        "lru_conv_b": nrm(ks[14], (DEPTH, LRU_WIDTH), 0.01),
        "lru_gate_w": nrm(ks[15], (DEPTH, 2, 2, LRU_BLOCKS, LRU_BS, LRU_BS), LRU_BS ** -0.5),
        "lru_gate_b": nrm(ks[16], (DEPTH, 2, 2, LRU_WIDTH), 0.01),
        "lru_lambda": lru_lambda,
        "na_rpb": nrm(ks[18], (DEPTH, NA_HEADS, 2 * NA_ROWS - 1, 2 * NA_COLS - 1), 0.1),
        "gqa_qk_g": 1.0 + nrm(ks[19], (DEPTH, 2, HEAD_DIM), 0.05),
        "w_out": nrm(ks[20], (DEPTH, MIX_WIDTH, D_MODEL), MIX_WIDTH ** -0.5),
        "w_ffn_in": nrm(ks[21], (DEPTH, D_MODEL, 2 * FFN_HIDDEN), D_MODEL ** -0.5),
        "w_ffn_out": nrm(ks[22], (DEPTH, FFN_HIDDEN, D_MODEL), FFN_HIDDEN ** -0.5),
    }

def reference(x_prompt, x_sample, cache_diff_kv, state_rglru, cache_na_kv, cache_gqa_kv,
              c, c_ctx, w_mod, b_mod, norm_g, w_in, diff_lambda_w, lru_conv_w, lru_conv_b,
              lru_gate_w, lru_gate_b, lru_lambda, na_rpb, gqa_qk_g, w_out, w_ffn_in, w_ffn_out):

    def diff_lambda(l):
        lq1, lk1, lq2, lk2 = diff_lambda_w[l].astype(jnp.float32)
        lam_init = 0.8 - 0.6 * math.exp(-0.3 * l)
        lam = jnp.exp(jnp.sum(lq1 * lk1)) - jnp.exp(jnp.sum(lq2 * lk2)) + lam_init
        return lam, lam_init

    def rglru(xb, gb, l, h0):
        return rglru_bidir(xb, gb, lru_conv_w[l], lru_conv_b[l], lru_gate_w[l], lru_gate_b[l],
                           lru_lambda[l], h0)

    def context_mixer(u, l):
        b, s = u.shape[:2]
        aq, ak, av, bx, bg, cq, ck, cv, dq, dk, dv = split_in(u)
        lam, lam_init = diff_lambda(l)
        va = av.reshape(b, s, DA_HEADS, HEAD_DIM)
        o_a = diff_attention(aq.reshape(b, s, DA_HEADS, 2, DA_DH), ak.reshape(b, s, DA_HEADS, 2, DA_DH),
                             va, lam, lam_init)
        kv_a = jnp.stack([ak.reshape(b, s, DA_HEADS, HEAD_DIM), va], axis=1)
        o_b, st_b = rglru(bx, bg, l, jnp.zeros((b, 2, LRU_WIDTH), jnp.float32))
        kc = ck.reshape(b, s, NA_HEADS, HEAD_DIM)
        vc = cv.reshape(b, s, NA_HEADS, HEAD_DIM)
        o_c = gqa_attention(cq.reshape(b, s, NA_HEADS, HEAD_DIM), kc, vc)
        kv_c = jnp.stack([kc, vc], axis=1)
        qd = rmsnorm(dq.reshape(b, s, GQA_Q_HEADS, HEAD_DIM), gqa_qk_g[l, 0])
        kd = rmsnorm(dk.reshape(b, s, GQA_KV_HEADS, HEAD_DIM), gqa_qk_g[l, 1])
        vd = dv.reshape(b, s, GQA_KV_HEADS, HEAD_DIM)
        o_d = gqa_attention(qd, kd, vd)
        kv_d = jnp.stack([kd, vd], axis=1)
        out = jnp.concatenate([o_a.reshape(b, s, -1), o_b, o_c.reshape(b, s, -1), o_d.reshape(b, s, -1)],
                              axis=-1)
        return out, (kv_a, st_b, kv_c, kv_d)

    def latent_mixer(u, l):
        b, n = u.shape[:2]
        p = cache_diff_kv.shape[3]
        aq, ak, av, bx, bg, cq, ck, cv, dq, dk, dv = split_in(u)
        lam, lam_init = diff_lambda(l)
        qa = axial_rope(aq.reshape(b, n, DA_HEADS, 2, DA_DH))
        ka = axial_rope(ak.reshape(b, n, DA_HEADS, 2, DA_DH))
        ka = jnp.concatenate([cache_diff_kv[:, l, 0].reshape(b, p, DA_HEADS, 2, DA_DH), ka], axis=1)
        va = jnp.concatenate([cache_diff_kv[:, l, 1], av.reshape(b, n, DA_HEADS, HEAD_DIM)], axis=1)
        o_a = diff_attention(qa, ka, va, lam, lam_init)
        o_b, _ = rglru(bx, bg, l, state_rglru[:, l])
        o_c = neighbourhood_attention(cq.reshape(b, n, NA_HEADS, HEAD_DIM), ck.reshape(b, n, NA_HEADS, HEAD_DIM),
                                      cv.reshape(b, n, NA_HEADS, HEAD_DIM),
                                      cache_na_kv[:, l, 0], cache_na_kv[:, l, 1], na_rpb[l])
        qd = axial_rope(rmsnorm(dq.reshape(b, n, GQA_Q_HEADS, HEAD_DIM), gqa_qk_g[l, 0]))
        kd = axial_rope(rmsnorm(dk.reshape(b, n, GQA_KV_HEADS, HEAD_DIM), gqa_qk_g[l, 1]))
        kd = jnp.concatenate([cache_gqa_kv[:, l, 0], kd], axis=1)
        vd = jnp.concatenate([cache_gqa_kv[:, l, 1], dv.reshape(b, n, GQA_KV_HEADS, HEAD_DIM)], axis=1)
        o_d = gqa_attention(qd, kd, vd)
        out = jnp.concatenate([o_a.reshape(b, n, -1), o_b, o_c.reshape(b, n, -1), o_d.reshape(b, n, -1)],
                              axis=-1)
        return out, None

    def layer(x, cond, l, mixer):
        mod = (jax.nn.silu(cond) @ w_mod[l] + b_mod[l])[:, None, :]
        sh_m, sc_m, g_m, sh_f, sc_f, g_f = jnp.split(mod, 6, axis=-1)
        h = rmsnorm(x, norm_g[l, 0]) * (1.0 + sc_m) + sh_m
        m, ctx_out = mixer(h @ w_in[l], l)
        x = x + g_m * rmsnorm(m @ w_out[l], norm_g[l, 1])
        h = rmsnorm(x, norm_g[l, 2]) * (1.0 + sc_f) + sh_f
        a, g = jnp.split(h @ w_ffn_in[l], 2, axis=-1)
        x = x + g_f * rmsnorm((jax.nn.silu(g) * a) @ w_ffn_out[l], norm_g[l, 3])
        return x, ctx_out

    y_prompt = x_prompt
    kv_a_list, st_list, kv_c_list, kv_d_list = [], [], [], []
    for l in range(DEPTH):
        y_prompt, (kv_a, st_b, kv_c, kv_d) = layer(y_prompt, c_ctx[None, :], l, context_mixer)
        kv_a_list.append(kv_a)
        st_list.append(st_b)
        kv_c_list.append(kv_c)
        kv_d_list.append(kv_d)
    new_cache_diff_kv = jnp.stack(kv_a_list, axis=1)
    new_state_rglru = jnp.stack(st_list, axis=1)
    new_cache_na_kv = jnp.stack(kv_c_list, axis=1)
    new_cache_gqa_kv = jnp.stack(kv_d_list, axis=1)

    y_sample = x_sample
    for l in range(DEPTH):
        y_sample, _ = layer(y_sample, c, l, latent_mixer)

    return (y_prompt, y_sample, new_cache_diff_kv, new_state_rglru, new_cache_na_kv, new_cache_gqa_kv)


_drawn_inputs = setup_inputs


def setup_inputs(seed=0):
    import zlib

    import numpy as np

    out = dict(_drawn_inputs(seed))
    spreads = {}
    factors = {'cache_na_kv': 3.62,
     'cache_gqa_kv': 7.195,
     'diff_lambda_w': 6.017,
     'lru_gate_b': 8.0,
     'na_rpb': 64.0,
     'cache_diff_kv': 8.0,
     'state_rglru': 6.765}
    for name, (base, spread) in spreads.items():
        noise = np.random.default_rng([zlib.crc32(name.encode()), seed]).standard_normal(out[name].shape)
        drawn = base * np.exp(spread * noise) if base else spread * noise
        out[name] = __import__('jax').numpy.asarray(drawn.astype(out[name].dtype))
    for name, factor in factors.items():
        out[name] = (out[name] * factor).astype(out[name].dtype)
    return out
```

```python
from contextlib import ExitStack

import numpy as np

import concourse.bass as bass
from concourse import mybir

F32 = mybir.dt.float32
F32R = mybir.dt.float32r
ALU = mybir.AluOpType
ACT = mybir.ActivationFunctionType
AX_X = mybir.AxisListType.X

P = 128
D = 2048
CTX, LAT = 128, 256
TB = (CTX + LAT) // P
T = CTX + LAT
KD = D // P
NC = 512
KG = 4
HD = 128
IN_W = 5120
IN_N = IN_W // NC
FFN = 5632
FFN_N = FFN // NC
FK = FFN // P
MOD_N = 6 * D // NC
EPS = 1e-6
LAM_INIT = 0.8 - 0.6 * 1.0
GRID_W = 64
BX, BG, AQ, AK, AV, CQ, CK, CV, DQ, DK, DV = 0, 512, 1024, 1536, 2048, 2560, 3072, 3584, 4096, 4608, 4864
RAW = 4
RING = 2
HK = KG // 2
MOD1 = 8
C_IN0 = MOD1 * KG
C_EL = C_IN0 + 2 * KG
EL = 3 * KG
N_EL = IN_N - 2
C_OUT = C_EL + N_EL * EL
C_F1 = C_OUT + D // NC * KG
C_F2 = C_F1 + 2 * FFN_N * KG
KG2 = FK // KG
N_TILES = C_F2 + D // NC * KG2
EL_PLAN = [("in", 0, 0), ("mod", 0, 0), ("mod", 0, 1), ("in", 0, 1), ("mod", 0, 2), ("mod", 0, 3),
           ("in", 0, 2), ("mod", 1, 0), ("mod", 1, 1), ("in", 0, 3), ("mod", 1, 2), ("mod", 1, 3)]
SH_M, SC_M, G_M, SH_F, SC_F, G_F = (KD * j for j in range(6))
XW = 392
LW = 388
L_LINKS = (3, 11)
L0 = CTX + 3
NA_OFF = 3
NA_RHO = 7
PADW = 48 + 31 + 48


def build(nc, wst, x_p, x_s, cdiff, state, cna, cgqa, c, c_ctx, b_mod, norm_g, lam_w, conv_w,
          conv_b, gate_w, gate_b, lru_lam, na_rpb, qk_g, ident_d, tables_d,
          y_p, y_s, o_diff, o_state, o_na, o_gqa):
    rpb_pad = nc.dram_tensor("rpb_pad", (GRID_W, 4 * NA_RHO * PADW), F32, kind="Internal").ap()
    x1_dram = nc.dram_tensor("x1_dram", (P, TB, D), F32, kind="Internal").ap()

    base = (nc.sbuf_base + 31) // 32 * 32
    X0 = 0
    RW0 = X0 + TB * D * 4
    HI0 = RW0 + RAW * KG * NC * 4
    LO0 = HI0 + RING * KG * NC * 4
    H0 = LO0 + RING * KG * NC * 4
    U0 = H0 + 2 * KD * T * 4
    P0 = U0 + FK * T * 4

    def at(name, shape, off, dt=F32):
        return nc.alloc_sbuf_tensor_at(name, shape, dt, offset=base + off)

    x_sb = at("x_sb", [P, TB, D], X0)
    slot = lambda name, s: at(name, [P, XW], X0 + s * XW * 4)
    XP, XC, BGT, GT, GG = (slot(n, s) for s, n in enumerate(("lru_xp", "lru_xc", "lru_bg", "lru_gt", "lru_gg")))
    RT = [slot(f"lru_rt{d}", 5 + d) for d in range(2)]
    AA = [slot(f"lru_aa{d}", 7 + d) for d in range(2)]
    TT = [slot(f"lru_tt{d}", 9 + d) for d in range(2)]
    II = [slot(f"lru_ii{d}", 11 + d) for d in range(2)]
    tables = at("tables", [P, 448], X0 + 20736)
    gbc = at("gbc", [P, 2, HD], X0 + 22528)
    lamw = at("lamw", [P, 4, 64], X0 + 23552)
    nabias = at("nabias", [P, 4, 2, 4, GRID_W], X0)
    kvA = at("kvA", [P, 2, 512], X0 + 8192)
    kvC = at("kvC", [P, 2, 512], X0 + 12288)
    kvD = at("kvD", [P, 2, 256], X0 + 16384)
    rows_st = at("rows_st", [8, P], X0 + 19968)
    sg = at("sg", [P, TB, NC], X0)
    h3 = at("h3", [P, TB, NC], X0 + 6144)
    raw = at("raw", [P, RAW, KG, NC], RW0)
    whi = at("whi", [P, 2 * RING, HK, NC], HI0, F32R)
    wlo = at("wlo", [P, 2 * RING, HK, NC], LO0, F32R)
    h_hi = at("h_hi", [P, KD, T], H0, F32R)
    h_lo = at("h_lo", [P, KD, T], H0 + KD * T * 4, F32R)
    j_hi = [at(f"j_hi{s}", [P, KG, T], H0 + s * 12288, F32R) for s in range(2)]
    j_lo = [at(f"j_lo{s}", [P, KG, T], H0 + s * 12288 + 6144, F32R) for s in range(2)]
    y2 = at("y2", [P, TB, D], H0 + KD * T * 4)
    ppad = at("ppad", [GRID_W, 4 * NA_RHO, PADW], H0)
    xn = at("xn", [P, TB, D], U0)
    xnT = at("xnT", [P, KD, T], U0 + TB * D * 4)
    dump = at("dump", [P, D], U0 + 2 * TB * D * 4)
    rows1 = at("rows1", [P, P], U0 + 57344)
    rows2 = at("rows2", [P, P], U0 + 57856)
    silu = at("silu", [P, 2, 2, KD], U0 + 58368)
    U = at("U", [P, TB, IN_W], U0)
    pool_t = at("pool_t", [P, 768], U0 + 61440)
    gw = at("gw", [P, 4, P], U0 + 64512)
    kT = [at(f"kT{s}", [P, 512], U0 + s * 2048) for s in range(2)]
    qT = [at(f"qT{s}", [P, T], U0 + 20480 + s * 1536) for s in range(2)]
    pT = [at(f"pT{s}", [P, T], U0 + 40960 + s * 1536) for s in range(2)]
    y1 = at("y1", [P, TB, D], U0)
    h3T = at("h3T", [P, FK, T], U0)
    ident = at("ident", [P, P], P0)
    ones = at("ones", [P, P], P0 + 512)
    pc1 = at("pc1", [P, P], P0 + 1024)
    pc2 = at("pc2", [P, P], P0 + 1536)
    modc = at("modc", [P, 96, 2], P0 + 2048)
    stat = at("stat", [P, KD, 4], P0 + 2816, F32R)
    diag = at("diag", [P, KG, P], P0 + 3072)
    modrow = at("modrow", [4, NC], P0 + 3072)
    prob = [[at("prob00", [P, T], U0 + 64512), at("prob01", [P, T], U0 + 66048)],
            [at("prob10", [P, T], X0 + 18432), at("prob11", [P, T], P0 + 3072)]]
    smalls = at("smalls", [P, 184], P0 + 5120)
    sm_at = [0]

    def small(name, n):
        sm_at[0] += n
        assert sm_at[0] <= 184
        return smalls[:, sm_at[0] - n:sm_at[0]]

    xss, xrs = small("xss", 3), small("xrs", 3)
    yss, yrs = small("yss", 12), small("yrs", 3)
    hb, sp4 = small("hb", 16), small("sp4", 8)
    stc = small("stc", 8)
    neglam, lamt = small("neglam", 1), small("lamt", 4)
    ssA, rsA = small("ssA", 12), small("rsA", 12)
    nds, negh = small("nds", 18), small("negh", 18)
    mxt, negm, psm, prc = small("mxt", 4), small("negm", 4), small("psm", 4), small("prc", 4)
    sel = small("sel", 2)
    spt = small("spt", 32)
    NG, CW, CB, GB, LL, ST = 0, 64, 80, 84, 100, 108

    with ExitStack() as ctx:
        ps = [ctx.enter_context(nc.psum_tensor(f"ps{b}", [P, NC], F32)) for b in range(8)]
        sem = lambda name: ctx.enter_context(nc.semaphore(name))
        raw_in = [sem(f"raw_in{s}") for s in range(RAW)]
        w_hi, w_lo, w_used = sem("w_hi"), sem("w_lo"), sem("w_used")
        par_in, par2_in, x_in, tab_in = sem("par_in"), sem("par2_in"), sem("x_in"), sem("tab_in")
        sel_ok, xp_zero = sem("sel_ok"), sem("xp_zero")
        sp_a, sp_e = sem("sp_a"), sem("sp_e")
        par_t, par_cp = sem("par_t"), sem("par_cp")
        silu_t, silu_f, stat_hi, stat_lo = sem("silu_t"), sem("silu_f"), sem("stat_hi"), sem("stat_lo")
        sq_done, rs_done, xn_done = sem("sq_done"), sem("rs_done"), sem("xn_done")
        xt_ps, xt_cp = sem("xt_ps"), sem("xt_cp")
        h_f, h_hs, h_ls = sem("h_f"), sem("h_hs"), sem("h_ls")
        mod_row, mod_sel, mod_col = sem("mod_row"), sem("mod_sel"), sem("mod_col")
        acc_free = sem("acc_free")
        l_setup, l_stage, gw_in = sem("l_setup"), sem("l_stage"), sem("gw_in")
        l_tr, l_xp, l_xc = sem("l_tr"), sem("l_xp"), sem("l_xc")
        l_gate, l_tanh, l_q, l_a, l_tq = sem("l_gate"), sem("l_tanh"), sem("l_q"), sem("l_a"), sem("l_tq")
        l_s, l_mu, l_ix = sem("l_s"), sem("l_mu"), sem("l_ix")
        l_g1, l_g2, l_gg, l_y = sem("l_g1"), sem("l_g2"), sem("l_gg"), sem("l_y")
        dch, pch = sem("dch"), sem("pch")
        lch = [sem(f"lch{e}") for e in range(2)]
        rpb_w, bias_in, kv_in, bias_ok = sem("rpb_w"), sem("bias_in"), sem("kv_in"), sem("bias_ok")
        lam_p, lam_e, lam_ok = sem("lam_p"), sem("lam_e"), sem("lam_ok")
        rope_ok = sem("rope_ok")
        mb_hi, mb_lo = sem("mb_hi"), sem("mb_lo")
        st_t, st_cp = sem("st_t"), sem("st_cp")
        prep_ps, prep_cp = sem("prep_ps"), sem("prep_cp")
        sc_ps, mx, ex, pr = sem("sc_ps"), sem("mx"), sem("ex"), sem("pr")
        pt_ps, pt_cp, pv_ps, o_hi, o_fr = sem("pt_ps"), sem("pt_cp"), sem("pv_ps"), sem("o_hi"), sem("o_fr")
        oa_cp, ra_ok, oa_sc, oa_ps, oa_hi, oa_lo = (sem(n) for n in ("oa_cp", "ra_ok", "oa_sc", "oa_ps", "oa_hi", "oa_lo"))
        dg_ok, g_ps, y_cp, y_g = sem("dg_ok"), sem("g_ps"), sem("y_cp"), sem("y_g")
        x1_ok, spill, x1_in = sem("x1_ok"), sem("spill"), sem("x1_in")
        s_tanh, s_silu, h3_ok, ht_ps, ht_cp = sem("s_tanh"), sem("s_silu"), sem("h3_ok"), sem("ht_ps"), sem("ht_cp")
        jh, jl = sem("jh"), sem("jl")
        fin = sem("fin")
        stored = sem("stored")
        block = ctx.enter_context(nc.Block())

        HEADS = [("A", h) for h in range(4)] + [("C", h) for h in range(4)] + [("D", h) for h in range(4)]
        UNITS = [(kind, h, tb) for kind, h in HEADS for tb in range(TB)]
        NU = len(UNITS)

        def width(tb):
            return P if tb == 0 else 3 * P

        def keys(tb):
            return slice(0, P) if tb == 0 else slice(P, 4 * P)

        def vblocks(kind, h, tb):
            col = {"A": AV + h * HD, "C": CV + h * HD, "D": DV + h // 2 * HD}[kind]
            if tb == 0:
                return [U[:, 0, col:col + HD]]
            hk = h if kind != "D" else h // 2
            cache = {"A": kvA, "C": kvC, "D": kvD}[kind][:, 1, hk * HD:(hk + 1) * HD]
            return [cache, U[:, 1, col:col + HD], U[:, 2, col:col + HD]]

        def nsoft(kind):
            return 2 if kind == "A" else 1

        KBASE = {"A": 0, "C": 8, "D": 12}


        def at_reg(start, n=1):
            return slice(start, start + n) if isinstance(start, int) else bass.ds(start, n)

        def tile_no(i, e, q):
            return i * (2 * EL) + (C_EL + e * EL + q)

        def in_banks(e):
            return 3 * e

        def xt_bank(k, done):
            return (3 + k % 5, 5) if done else (k % 6, 6)

        @block.sync
        def _(sp):
            sp.dma_start(rows1[0:16, :], c.rearrange("a (k p) -> (a k) p", p=P)).then_inc(par_in, 16)
            sp.dma_start(rows1[16:32, :], c_ctx.rearrange("(k p) -> k p", p=P)).then_inc(par_in, 16)
            sp.dma_start(rows1[32:128, :], b_mod.rearrange("a (k p) -> (a k) p", p=P)).then_inc(par_in, 16)
            sp.dma_start(ident[:, :], ident_d).then_inc(par_in, 16)
            for s in range(RAW):
                sp.dma_start(raw[:, s].rearrange("p k n -> p (k n)"), wst[s]).then_inc(raw_in[s], 16)
            with sp.Fori(1, N_TILES // RAW) as i:
                for s in range(RAW):
                    sp.wait_ge(w_lo, i * (2 * RAW) + (2 * (s + 1) - 2 * RAW))
                    sp.dma_start(raw[:, s].rearrange("p k n -> p (k n)"), wst[i * RAW + s]).then_inc(raw_in[s], 16)

        @block.scalar
        def _(act):
            def hi(t, s, fills):
                act.wait_ge(raw_in[s], fills * 16)
                for b in range(2):
                    if not (isinstance(t, int) and t < RING):
                        act.wait_ge(w_used, t * 2 + (b + 1 - 2 * RING))
                    nc.scalar.activation(whi[:, s % RING * 2 + b], raw[:, s, HK * b:HK * b + HK], ACT.Copy)\
                        .then_inc(w_hi, 1)

            def hi_at(t):
                hi(t, t % RAW, t // RAW + 1)

            def hi_el(i, e, q):
                c0 = C_EL + e * EL + q
                hi(i * (2 * EL) + c0, c0 % RAW, i * (2 * EL // RAW) + (c0 // RAW + 1))

            def rows_out(n, last_tile, bank):
                act.wait_ge(w_used, last_tile * 2 + 2)
                if not (isinstance(n, int) and n == 0):
                    act.wait_ge(mod_sel, n)
                nc.scalar.activation(modrow[:, :], ps[bank][0:4, :], ACT.Copy).then_inc(mod_row, 1)

            def cols_out(n, bank):
                act.wait_ge(mod_sel, n + 1)
                nc.scalar.activation(modc[:, at_reg(n * 4, 4), :],
                                     ps[bank][:, 0:8].rearrange("p (f j) -> p f j", j=2), ACT.Copy)\
                    .then_inc(mod_col, 1)

            def u_out(n, last_tile, bank):
                act.wait_ge(w_used, last_tile * 2 + 2)
                for tb in range(TB):
                    ins = nc.scalar.activation(U[:, tb, at_reg(n * NC, NC)], ps[bank + tb][:, :], ACT.Copy)
                ins.then_inc(acc_free, 1)

            act.sem_inc(ht_cp, 1)
            act.dma_start(x_sb[:, 0, :], x_p.rearrange("a s d -> (a s) d")).then_inc(x_in, 16)
            act.dma_start(x_sb[:, 1:3, :], x_s.rearrange("a (t p) d -> p (a t) d", p=P)).then_inc(x_in, 16)
            row = 0
            for src in (norm_g.rearrange("a j (k p) -> (a j k) p", p=P),
                        conv_w.rearrange("a j (k p) -> (a j k) p", p=P),
                        conv_b.rearrange("a (k p) -> (a k) p", p=P),
                        gate_b.rearrange("a d g (k p) -> (a d g k) p", p=P),
                        lru_lam.rearrange("a d (k p) -> (a d k) p", p=P),
                        state.rearrange("b a d (k p) -> (b a d k) p", p=P)):
                act.dma_start(rows2[row:row + src.shape[0], :], src).then_inc(par2_in, 16)
                row += src.shape[0]
            act.wait_ge(par_t, 1)
            nc.scalar.activation(pc1[:, :], ps[4][:, 0:128], ACT.Copy).then_inc(par_cp, 1)
            act.wait_ge(par_cp, 1)
            nc.scalar.activation(silu[:, 0].rearrange("p j k -> p (j k)"), pc1[:, 0:32], ACT.Tanh,
                                 scale=0.5).then_inc(silu_t, 1)
            act.wait_ge(silu_f, 1)
            nc.scalar.activation(stat[:, :, 0:2].rearrange("p k j -> p j k"), silu[:, 1], ACT.Copy).then_inc(stat_hi, 1)
            act.wait_ge(par_t, 2)
            nc.scalar.activation(pc2[:, 0:116], ps[5][:, 0:116], ACT.Copy).then_inc(par_cp, 1)
            act.wait_ge(sp_a, 1)
            nc.scalar.activation(spt[:, 8:16], spt[:, 0:8], ACT.Exp, scale=-1.0).then_inc(sp_e, 1)

            def squares(done):
                for tb in range(TB):
                    if tb:
                        act.wait_ge(sq_done, done + tb)
                    nc.scalar.activation(dump[:, :], x_sb[:, tb, :], ACT.Square,
                                         accum_out=xss[:, tb:tb + 1]).then_inc(sq_done, 1)

            for n in range(2):
                hi_at(4 * n)
                if n:
                    rows_out(n - 1, 4 * n - 1, 6 + (n - 1) % 2)
                hi_at(4 * n + 1)
                hi_at(4 * n + 2)
                if n:
                    cols_out(n - 1, 6 + (n - 1) % 2)
                hi_at(4 * n + 3)
                if n == 0:
                    act.wait_ge(x_in, 32)
                    squares(0)
            with act.Fori(1, MOD1 // 2) as i:
                for half in range(2):
                    n, bank = i * 2 + half, 6 + (half + 1) % 2
                    hi(i * 8 + 4 * half, 0, i * 2 + (half + 1))
                    rows_out(i * 2 + (half - 1), i * 8 + (4 * half - 1), bank)
                    hi(i * 8 + (4 * half + 1), 1, i * 2 + (half + 1))
                    hi(i * 8 + (4 * half + 2), 2, i * 2 + (half + 1))
                    cols_out(i * 2 + (half - 1), bank)
                    hi(i * 8 + (4 * half + 3), 3, i * 2 + (half + 1))
            hi_at(C_IN0)
            rows_out(MOD1 - 1, C_IN0 - 1, 7)
            cols_out(MOD1 - 1, 7)
            hi_at(C_IN0 + 1)

            def h_high(ks, done):
                for k in ks:
                    act.wait_ge(h_f, done + k + 1)
                    nc.scalar.activation(h_hi[:, k, :], xnT[:, k, :], ACT.Copy).then_inc(h_hs, 1)

            act.wait_ge(rpb_w, 80)
            h_high(range(8), 0)
            hi_at(C_IN0 + 2)
            h_high(range(8, 12), 0)
            hi_at(C_IN0 + 3)
            h_high(range(12, 16), 0)
            hi_at(C_IN0 + 4)
            u_out(0, C_IN0 + 3, 0)
            for q in range(5, 8):
                hi_at(C_IN0 + q)

            def element(i, e, first):
                n = i * 4 + (MOD1 + 2 * e)
                last = tile_no(i, e, -1)
                hi_el(i, e, 0)
                u_out(i * 2 + (1 + e), last if first else tile_no(i, e, -3), in_banks(1 - e))
                if not first:
                    rows_out(i * 4 + (MOD1 + 2 * e - 1), last, 7)
                hi_el(i, e, 1)
                hi_el(i, e, 2)
                if not first:
                    cols_out(i * 4 + (MOD1 + 2 * e - 1), 7)
                hi_el(i, e, 3)
                hi_el(i, e, 4)
                if e == 1:
                    for g in range(3):
                        gate_tanh(i, g)
                hi_el(i, e, 5)
                hi_el(i, e, 6)
                rows_out(n, tile_no(i, e, 5), 6)
                if e == 1:
                    for d in range(2):
                        act.wait_ge(l_q, i * 2 + (d + 1))
                        nc.scalar.activation(AA[d][:, 0:LW], RT[d][:, 0:LW], ACT.Exp, scale=-1.0).then_inc(l_a, 1)
                        nc.scalar.activation(TT[d][:, 0:LW], RT[d][:, 0:LW], ACT.Tanh).then_inc(l_tq, 1)
                hi_el(i, e, 7)
                if e == 0:
                    act.wait_ge(l_tr, i + 1)
                    act.wait_ge(xp_zero, 1)
                    nc.scalar.activation(XP[:, 2:2 + CTX], ps[3][:, 0:CTX], ACT.Copy)
                    nc.scalar.activation(XP[:, 2 + L0:2 + L0 + LAT], ps[3][:, CTX:T], ACT.Copy)
                    nc.scalar.activation(BGT[:, 0:T], ps[4][:, 0:T], ACT.Copy).then_inc(l_xp, 1)
                else:
                    gate_tanh(i, 3)
                hi_el(i, e, 8)
                cols_out(n, 6)
                if e == 1:
                    for d in range(2):
                        act.wait_ge(l_s, i * 2 + (d + 1))
                        nc.scalar.activation(TT[d][:, 0:LW], TT[d][:, 0:LW], ACT.Sqrt, scale=2.0).then_inc(l_mu, 1)
                hi_el(i, e, 9)
                hi_el(i, e, 10)
                if e == 0:
                    act.wait_ge(l_g1, i + 1)
                    nc.scalar.activation(GG[:, 0:T], GT[:, 0:T], ACT.Tanh, scale=0.7978845608028654).then_inc(l_g2, 1)
                hi_el(i, e, 11)

            def gate_tanh(i, g):
                d, kind = g % 2, g // 2
                act.wait_ge(l_gate, i * 4 + (g + 1))
                nc.scalar.activation((RT, II)[kind][d][:, 0:LW], ps[g % 3][:, 0:LW], ACT.Tanh,
                                     bias=hb[:, at_reg(i + (8 * d + 4 * kind))], scale=0.5).then_inc(l_tanh, 1)

            act.wait_ge(l_setup, 2)
            for e in range(2):
                element(0, e, e == 0)
            with act.Fori(1, N_EL // 2) as i:
                for e in range(2):
                    element(i, e, False)

            u_out(IN_N - 1, C_OUT - 3, 3)
            rows_out(MOD_N - 1, C_OUT - 1, 7)
            cols_out(MOD_N - 1, 7)
            act.wait_ge(l_y, 4)
            for n in range(4):
                nc.scalar.activation(h_hi[:, 4 + n, :].rearrange("p (t f) -> p t f", f=P),
                                     U[:, :, n * P:(n + 1) * P], ACT.Copy).then_inc(mb_hi, 1)
            act.wait_ge(lam_p, 1)
            nc.scalar.activation(lamt[:, 2:4], lamt[:, 0:2], ACT.Exp).then_inc(lam_e, 1)
            act.wait_ge(st_t, 1)
            nc.scalar.activation(rows_st[0:8, :], ps[2][0:8, 0:P], ACT.Copy).then_inc(st_cp, 1)

            def prep_out(hd):
                act.wait_ge(prep_ps, hd + 1)
                if hd < 2:
                    act.wait_ge(mb_lo, 4)
                else:
                    act.wait_ge(sc_ps, TB * (hd - 1))
                nc.scalar.activation(qT[hd % 2][:, :], ps[0][:, 0:T], ACT.Copy)
                nc.scalar.activation(kT[hd % 2][:, :], ps[1][:, :], ACT.Copy).then_inc(prep_cp, 1)

            def o_high(u):
                kind, h, tb = UNITS[u]
                act.wait_ge(pv_ps, u + 1)
                if kind == "A":
                    act.wait_ge(oa_cp, u + 1)
                    nc.scalar.activation(ps[7][:, 0:P], ps[7][:, 0:P], ACT.Square,
                                         accum_out=ssA[:, u:u + 1]).then_inc(o_fr, 1)
                else:
                    nc.scalar.activation(h_hi[:, KBASE[kind] + h, tb * P:(tb + 1) * P],
                                         ps[7][:, 0:P], ACT.Copy).then_inc(o_hi, 1)

            prep_out(0)
            for s in range(NU + 4):
                if s == NU - 2:
                    hi_at(C_OUT)
                    hi_at(C_OUT + 1)
                if 4 <= s:
                    o_high(s - 4)
                if s < NU:
                    kind, h, tb = UNITS[s]
                    w = width(tb)
                    if tb == 1 and s // TB + 1 < len(HEADS):
                        prep_out(s // TB + 1)
                    act.wait_ge(mx, s + 1)
                    if s >= 2:
                        act.wait_ge(pt_ps, s - 1)
                    if s == 0:
                        act.wait_ge(mod_sel, MOD_N)
                    for j in range(nsoft(kind)):
                        local = kind == "C" and tb > 0
                        pr_b = prob[s % 2][j]
                        ins = nc.scalar.activation(pr_b[:, 0:w],
                                                   pr_b[:, 0:w] if local else ps[2 + 2 * (s % 2) + j][:, 0:w], ACT.Exp,
                                                   bias=negm[:, 2 * (s % 2) + j:2 * (s % 2) + j + 1],
                                                   scale=1.0 if local else (0.125 if kind == "A" else HD ** -0.5),
                                                   accum_out=psm[:, 2 * (s % 2) + j:2 * (s % 2) + j + 1])
                    ins.then_inc(ex, 1)
                if 2 <= s < NU + 2:
                    u = s - 2
                    act.wait_ge(pt_ps, u + 1)
                    if u >= 2:
                        act.wait_ge(pv_ps, u - 1)
                    w = width(UNITS[u][2])
                    nc.scalar.activation(pT[u % 2][:, 0:w], ps[6][:, 0:w], ACT.Copy).then_inc(pt_cp, 1)
            for h in range(4):
                act.wait_ge(oa_ps, h + 1)
                nc.scalar.activation(h_hi[:, h, :], ps[h][:, 0:T], ACT.Copy).then_inc(oa_hi, 1)

            act.wait_ge(stored, 7 * 16)

            def y_out(y, n, last_tile, bank):
                act.wait_ge(w_used, last_tile * 2 + 2)
                for tb in range(TB):
                    nc.scalar.activation(y[:, tb, n * NC:(n + 1) * NC], ps[bank + tb][:, :], ACT.Copy).then_inc(y_cp, 1)
                    ins = nc.scalar.activation(ps[bank + tb][:, :], ps[bank + tb][:, :], ACT.Square,
                                               accum_out=yss[:, 4 * tb + n:4 * tb + n + 1])
                ins.then_inc(acc_free, 1)

            for n in range(4):
                for q in range(KG):
                    if n or q > 1:
                        hi_at(C_OUT + 4 * n + q)
                    if q == 0 and n:
                        y_out(y1, n - 1, C_OUT + 4 * n - 1, 3 * ((n - 1) % 2))
            hi_at(C_F1)
            y_out(y1, 3, C_F1 - 1, 3)
            hi_at(C_F1 + 1)
            act.wait_ge(x1_ok, 3)
            squares(3)
            h_high(range(8), KD)
            hi_at(C_F1 + 2)
            h_high(range(8, 12), KD)
            hi_at(C_F1 + 3)
            h_high(range(12, 16), KD)

            def ht_out(j, f):
                act.wait_ge(ht_ps, j * 4 + (f + 2))
                nc.scalar.activation(h3T[:, at_reg(j * 4 + f), :].rearrange("p a t -> p (a t)"), ps[6 + f % 2][:, 0:T],
                                     ACT.Copy).then_inc(ht_cp, 1)

            def ffn_in(j, first):
                def hi_j(q):
                    t = C_F1 + q
                    hi(j * 8 + t, t % RAW, j * 2 + (t // RAW + 1))
                if not first:
                    hi_j(0)
                    hi_j(1)
                    hi_j(2)
                    ht_out(j - 1, 0)
                    ht_out(j - 1, 1)
                    hi_j(3)
                    ht_out(j - 1, 2)
                    ht_out(j - 1, 3)
                hi_j(4)
                act.wait_ge(w_used, j * 16 + 2 * (C_F1 + 4))
                if first:
                    act.wait_ge(spill, 16)
                else:
                    act.wait_ge(h3_ok, j)
                for tb in range(TB):
                    nc.scalar.activation(sg[:, tb, :], ps[tb][:, :], ACT.Tanh, scale=0.5).then_inc(s_tanh, 1)
                for q in (5, 6, 7):
                    hi_j(q)

            ffn_in(0, True)
            with act.Fori(1, FFN_N) as j:
                ffn_in(j, False)

            for n in range(4):
                for q in range(KG2):
                    t = C_F2 + n * KG2 + q
                    hi_at(t)
                    if n == 0 and q == 0:
                        for f in range(4):
                            ht_out(FFN_N - 1, f)
                    act.wait_ge(w_used, 2 * (t - 1))
                    nc.scalar.activation(j_hi[t % 2][:, :, :], h3T[:, KG * q:KG * q + KG, :], ACT.Copy).then_inc(jh, 1)
                    if q == 1 and n:
                        y_out(y2, n - 1, C_F2 + n * KG2 - 1, 3 * ((n - 1) % 2))
            y_out(y2, 3, N_TILES - 1, 3)

        @block.tensor
        def _(pe):
            def halves(t, s):
                for b in range(2):
                    pe.wait_ge(w_lo, t * 2 + (b + 1))
                    yield b, whi[:, 2 * s + b], wlo[:, 2 * s + b]

            def mod_tile(t, s, kg, bank):
                for b, wh, wl in halves(t, s):
                    for kk in range(HK):
                        k = KG * kg + HK * b + kk
                        nc.tensor.matmul(ps[bank][0:4, :], stat[:, k, :], wh[:, kk, :], start=(k == 0), stop=False)
                        ins = nc.tensor.matmul(ps[bank][0:4, :], stat[:, k, :], wl[:, kk, :],
                                               start=False, stop=(k == KD - 1))
                    ins.then_inc(w_used, 1)

            def proj_tile(t, s, kg, bank, xh, xl, k_last, ready=None):
                for b, wh, wl in halves(t, s):
                    for kk in range(HK):
                        k = KG * kg + HK * b + kk
                        if ready is not None:
                            pe.wait_ge(h_ls, ready + k + 1)
                        for tb in range(TB):
                            xs = slice(tb * P, (tb + 1) * P)
                            acc = ps[bank + tb][:, :]
                            nc.tensor.matmul(acc, xh[:, kk + HK * b, xs], wh[:, kk, :], start=(k == 0), stop=False)
                            nc.tensor.matmul(acc, xl[:, kk + HK * b, xs], wh[:, kk, :], start=False, stop=False)
                            ins = nc.tensor.matmul(acc, xh[:, kk + HK * b, xs], wl[:, kk, :],
                                                   start=False, stop=(k == k_last))
                    ins.then_inc(w_used, 1)

            def h_tile(t, s, kg, bank, ready=None):
                proj_tile(t, s, kg, bank, h_hi[:, KG * kg:KG * kg + KG], h_lo[:, KG * kg:KG * kg + KG], KD - 1, ready)

            def mod_select(n, bank):
                pe.wait_ge(mod_row, n + 1)
                for f in range(4):
                    ins = nc.tensor.matmul(ps[bank][:, 2 * f:2 * f + 2], modrow[:, f * P:(f + 1) * P], sel[0:4, :],
                                           start=(f == 0), stop=(f == 3), skip_group_check=True)
                ins.then_inc(mod_sel, 1)

            def x_transposes(ks, done):
                for k in ks:
                    bank, lag = xt_bank(k, done)
                    if k >= lag:
                        pe.wait_ge(h_f if done else xt_cp, done + k - lag + 1)
                    for tb in range(TB):
                        ins = nc.tensor.transpose(ps[bank][:, tb * P:(tb + 1) * P], xn[:, tb, k * P:(k + 1) * P], ident[:, :])
                    ins.then_inc(xt_ps, 1)

            pe.sem_inc(ht_ps, 1)
            pe.wait_ge(par_in, 64)
            nc.tensor.transpose(ps[4][:, 0:128], rows1[:, :], ident[:, :]).then_inc(par_t, 1)
            pe.wait_ge(par2_in, 96)
            nc.tensor.transpose(ps[5][:, 0:116], rows2[0:116, :], ident[0:116, 0:116]).then_inc(par_t, 1)
            pe.wait_ge(stat_lo, 1)
            pe.wait_ge(sel_ok, 1)
            for n in range(2):
                for kg in range(KG):
                    mod_tile(4 * n + kg, kg % RING, kg, 6 + n % 2)
                    if n and kg == 0:
                        mod_select(n - 1, 6 + (n - 1) % 2)
            pe.wait_ge(par_cp, 2)
            pe.wait_ge(xn_done, TB)
            x_transposes(range(KD), 0)
            with pe.Fori(1, MOD1 // 2) as i:
                for half in range(2):
                    pe.wait_ge(mod_col, i * 2 + (half - 1))
                    for kg in range(KG):
                        mod_tile(i * 8 + (4 * half + kg), kg % RING, kg, 6 + half)
                        if kg == 0:
                            mod_select(i * 2 + (half - 1), 6 + (half + 1) % 2)
            mod_select(MOD1 - 1, 7)
            pe.wait_ge(xt_cp, KD)
            for n in range(2):
                for kg in range(KG):
                    h_tile(C_IN0 + 4 * n + kg, kg % RING, kg, 3 * n, 0 if n == 0 else None)

            def element(i, e, first):
                n = i * 4 + (MOD1 + 2 * e)
                pe.wait_ge(acc_free, i * 2 + (1 + e))
                if e == 1:
                    pe.wait_ge(l_xp, i + 1)
                elif not first:
                    pe.wait_ge(l_tanh, i * 4)
                for q, (what, m, kg) in enumerate(EL_PLAN):
                    t, s = tile_no(i, e, q), q % RING
                    if what == "in":
                        h_tile(t, s, kg, in_banks(e))
                    else:
                        if kg == 0:
                            pe.wait_ge(mod_col, n + (m - 1))
                        mod_tile(t, s, kg, 6 + m)
                    if q == 0 and not first:
                        mod_select(i * 4 + (MOD1 + 2 * e - 1), 7)
                    if q == 6:
                        mod_select(n, 6)
                    if q == 2 and e == 1:
                        pe.wait_ge(acc_free, i * 2 + 3)
                        pe.wait_ge(l_xc, i + 1)
                        pe.wait_ge(gw_in, i * 16 + 16)
                        for g in range(3):
                            gate(g)
                    if q == 5 and e == 1:
                        pe.wait_ge(l_tanh, i * 4 + 1)
                        gate(3)
                    if q == 5 and e == 0:
                        pe.wait_ge(acc_free, i * 2 + 2)
                        pe.wait_ge(l_stage, i + 1)
                        for src, b in ((AA[0], 3), (AA[1], 4)):
                            for tb in range(TB):
                                ins = nc.tensor.transpose(ps[b][:, tb * P:(tb + 1) * P],
                                                          src[:, tb * P:(tb + 1) * P], ident[:, :])
                        ins.then_inc(l_tr, 1)

            def gate(g):
                d, kind = g % 2, g // 2
                nc.tensor.matmul(ps[g % 3][:, 0:LW], gw[:, 2 * d + kind, :], XC[:, 0:LW], start=True, stop=True)\
                    .then_inc(l_gate, 1)

            for e in range(2):
                element(0, e, e == 0)
            with pe.Fori(1, N_EL // 2) as i:
                for e in range(2):
                    element(i, e, False)
            mod_select(MOD_N - 1, 7)

            pe.wait_ge(acc_free, IN_N)
            pe.wait_ge(l_tanh, 16)
            pe.wait_ge(l_y, 4)
            nc.tensor.transpose(ps[2][0:8, 0:P], stc[:, :], ident[:, :]).then_inc(st_t, 1)

            def prep(hd):
                kind, h = HEADS[hd]
                if hd:
                    pe.wait_ge(prep_cp, hd)
                if kind == "A" and h == 0:
                    pe.wait_ge(rope_ok, 1)
                    pe.wait_ge(kv_in, 48)
                if kind == "D" and h == 0:
                    pe.wait_ge(rope_ok, 2)
                qc = {"A": AQ, "C": CQ, "D": DQ}[kind] + h * HD
                hk = h // 2 if kind == "D" else h
                kc = {"A": AK, "C": CK, "D": DK}[kind] + hk * HD
                cache = {"A": kvA, "C": kvC, "D": kvD}[kind][:, 0, hk * HD:(hk + 1) * HD]
                for tb in range(TB):
                    nc.tensor.transpose(ps[0][:, tb * P:(tb + 1) * P], U[:, tb, qc:qc + HD], ident[:, :])
                for n, src in enumerate((U[:, 0, kc:kc + HD], cache, U[:, 1, kc:kc + HD], U[:, 2, kc:kc + HD])):
                    ins = nc.tensor.transpose(ps[1][:, n * P:(n + 1) * P], src, ident[:, :])
                ins.then_inc(prep_ps, 1)

            def scores(u):
                kind, h, tb = UNITS[u]
                hd = u // TB
                pe.wait_ge(prep_cp, hd + 1)
                if u >= 2:
                    pe.wait_ge(ex, u - 1)
                if u == 0:
                    pe.wait_ge(st_cp, 1)
                for j in range(nsoft(kind)):
                    part = slice(64 * j, 64 * j + 64) if kind == "A" else slice(0, P)
                    ins = nc.tensor.matmul(ps[2 + 2 * (u % 2) + j][:, 0:width(tb)], qT[hd % 2][part, tb * P:(tb + 1) * P],
                                           kT[hd % 2][part, keys(tb)], start=True, stop=True)
                ins.then_inc(sc_ps, 1)

            def p_transposes(u):
                tb = UNITS[u][2]
                pe.wait_ge(pr, u + 1)
                if u:
                    pe.wait_ge(pt_cp, u)
                for n in range(width(tb) // P):
                    ins = nc.tensor.transpose(ps[6][:, n * P:(n + 1) * P], prob[u % 2][0][:, n * P:(n + 1) * P], ident[:, :])
                ins.then_inc(pt_ps, 1)

            def values(u):
                kind, h, tb = UNITS[u]
                pe.wait_ge(pt_cp, u + 1)
                if u:
                    pe.wait_ge(o_fr, u)
                blocks = vblocks(kind, h, tb)
                for n, v in enumerate(blocks):
                    pt = pT[u % 2][:, n * P:(n + 1) * P]
                    lhs, rhs = (pt, v) if kind == "A" else (v, pt)
                    ins = nc.tensor.matmul(ps[7][:, 0:P], lhs, rhs, start=(n == 0), stop=(n == len(blocks) - 1))
                ins.then_inc(pv_ps, 1)

            prep(0)
            for s in range(NU + 3):
                if s < NU:
                    if s % TB == 1 and s // TB + 1 < len(HEADS):
                        prep(s // TB + 1)
                    scores(s)
                if 2 <= s < NU + 2:
                    p_transposes(s - 2)
                if s >= 3:
                    values(s - 3)
            pe.wait_ge(oa_sc, 12)
            pe.wait_ge(prep_cp, len(HEADS))
            pe.wait_ge(ex, NU)
            for h in range(4):
                for tb in range(TB):
                    ins = nc.tensor.transpose(ps[h][:, tb * P:(tb + 1) * P], U[:, tb, AQ + h * HD:AQ + (h + 1) * HD], ident[:, :])
                ins.then_inc(oa_ps, 1)

            def gains(idx, bank):
                pe.wait_ge(dg_ok, idx + 1)
                if idx >= 2:
                    pe.wait_ge(y_g, 3 * (idx // 2))
                nc.tensor.matmul(ps[bank][:, :], ones[:, :], diag[:, :, :].rearrange("p f n -> p (f n)"),
                                 start=True, stop=True).then_inc(g_ps, 1)

            pe.wait_ge(oa_lo, 4)
            pe.wait_ge(o_fr, NU)
            pe.wait_ge(mb_lo, 4)
            for n in range(4):
                pe.wait_ge(acc_free, IN_N + n - 1)
                for kg in range(KG):
                    h_tile(C_OUT + 4 * n + kg, kg % RING, kg, 3 * (n % 2))
                    if kg in (1, 3):
                        gains(2 * n + kg // 2, 7 - kg // 2)
            pe.wait_ge(acc_free, IN_N + 4)
            pe.wait_ge(xn_done, 2 * TB)
            x_transposes(range(8), KD)

            def h3_transposes(j, pair):
                pe.wait_ge(h3_ok, j + 1)
                pe.wait_ge(ht_cp, j * 4 + (2 * pair + 1))
                for f in (2 * pair, 2 * pair + 1):
                    for tb in range(TB):
                        ins = nc.tensor.transpose(ps[6 + f % 2][:, tb * P:(tb + 1) * P], h3[:, tb, f * P:(f + 1) * P], ident[:, :])
                    ins.then_inc(ht_ps, 1)

            def ffn_in(j, first):
                for part in range(2):
                    if not first:
                        pe.wait_ge((s_silu, h3_ok)[part], j)
                    for kg in range(KG):
                        h_tile(j * 8 + (C_F1 + 4 * part + kg), kg % RING, kg, 3 * part, KD if first and part == 0 else None)
                        if part == 0 and first and kg < 2:
                            x_transposes(range(4 * kg + 8, 4 * kg + 12), KD)
                        if part == 0 and not first and kg in (1, 2):
                            h3_transposes(j - 1, kg - 1)

            ffn_in(0, True)
            with pe.Fori(1, FFN_N) as j:
                ffn_in(j, False)

            h3_transposes(FFN_N - 1, 0)
            h3_transposes(FFN_N - 1, 1)
            pe.wait_ge(s_silu, FFN_N)
            with pe.Fori(0, 2) as i:
                for n2 in range(2):
                    pe.wait_ge(acc_free, i * 2 + (IN_N + 4 + n2 - 1))
                    for q in range(KG2):
                        t0 = n2 * KG2 + q
                        pe.wait_ge(jl, i * (2 * KG2) + (t0 + 1))
                        proj_tile(i * (2 * KG2) + (C_F2 + t0), t0 % RING, q, 3 * n2, j_hi[t0 % RING], j_lo[t0 % RING], FK - 1)
                        if q in (4, 8):
                            g = q // 4 - 1
                            pe.wait_ge(dg_ok, i * 4 + (8 + 2 * n2 + g + 1))
                            pe.wait_ge(y_g, i * 6 + (12 + 3 * n2))
                            nc.tensor.matmul(ps[7 - g][:, :], ones[:, :], diag[:, :, :].rearrange("p f n -> p (f n)"),
                                             start=True, stop=True).then_inc(g_ps, 1)

        @block.vector
        def _(dve):
            count = [0]

            def link(ins):
                count[0] += 1
                ins.then_inc(dch, 1)
                dve.wait_ge(dch, count[0])

            def lo(t, s):
                for b in range(2):
                    dve.wait_ge(w_hi, t * 2 + (b + 1))
                    nc.vector.tensor_tensor(wlo[:, s % RING * 2 + b], raw[:, s, HK * b:HK * b + HK],
                                            whi[:, s % RING * 2 + b].bitcast(F32), ALU.subtract).then_inc(w_lo, 1)

            def lo_at(t):
                lo(t, t % RAW)

            def lo_el(i, e, q):
                lo(tile_no(i, e, q), (C_EL + e * EL + q) % RAW)

            V = nc.vector
            dve.wait_ge(silu_t, 1)
            link(V.scalar_tensor_tensor(silu[:, 1].rearrange("p j k -> p (j k)"), silu[:, 0].rearrange("p j k -> p (j k)"),
                                        1.0, pc1[:, 0:32], ALU.add, ALU.mult))
            V.tensor_scalar(silu[:, 1].rearrange("p j k -> p (j k)"), silu[:, 1].rearrange("p j k -> p (j k)"),
                            0.5, None, ALU.mult).then_inc(silu_f, 1)
            dve.wait_ge(stat_hi, 1)
            V.tensor_tensor(stat[:, :, 2:4].rearrange("p k j -> p j k"), silu[:, 1],
                            stat[:, :, 0:2].rearrange("p k j -> p j k").bitcast(F32), ALU.subtract).then_inc(stat_lo, 1)
            V.tensor_tensor(sel[0:4, :], ident[0:4, 0:2], ident[0:4, 2:4], ALU.add).then_inc(sel_ok, 1)
            dve.wait_ge(par_cp, 2)
            V.tensor_scalar(hb[:, :], pc2[:, GB:GB + 16], 0.5, None, ALU.mult).then_inc(l_setup, 1)
            V.scalar_tensor_tensor(spt[:, 0:8], pc2[:, LL:LL + 8], -1.0, pc2[:, LL:LL + 8], ALU.mult, ALU.max).then_inc(sp_a, 1)

            for q in range(4):
                lo_at(q)
            dve.wait_ge(sp_e, 1)
            e8, z8, w8 = spt[:, 8:16], spt[:, 16:24], spt[:, 24:32]
            link(V.tensor_scalar(z8, e8, 2.0, None, ALU.add))
            link(V.reciprocal(z8, z8))
            link(V.tensor_tensor(z8, z8, e8, ALU.mult))
            link(V.tensor_tensor(w8, z8, z8, ALU.mult))
            link(V.tensor_scalar(e8, w8, 1.0 / 17, 1.0 / 15, ALU.mult, ALU.add))
            for m in (13, 11, 9, 7, 5, 3, 1):
                link(V.tensor_tensor(e8, e8, w8, ALU.mult))
                link(V.tensor_scalar(e8, e8, 1.0 / m, None, ALU.add))
            link(V.tensor_tensor(e8, e8, z8, ALU.mult))
            link(V.tensor_scalar(w8, pc2[:, LL:LL + 8], -1.0, 0.0, ALU.mult, ALU.max))
            link(V.scalar_tensor_tensor(sp4[:, :], e8, 2.0, w8, ALU.mult, ALU.add))
            V.tensor_scalar(sp4[:, :], sp4[:, :], 4.0, None, ALU.mult).then_inc(l_setup, 1)

            def normed():
                dve.wait_ge(rs_done, rs_count[0])
                for tb in range(TB):
                    V.tensor_scalar(xn[:, tb, :], x_sb[:, tb, :], xrs[:, tb:tb + 1], None, ALU.mult).then_inc(xn_done, 1)

            rs_count = [1]
            normed()
            for q in range(4, 8):
                lo_at(q)
            for k in range(KD):
                dve.wait_ge(xt_ps, k + 1)
                V.tensor_copy(xnT[:, k, :], ps[xt_bank(k, 0)[0]][:, 0:T]).then_inc(xt_cp, 1)
            with dve.Fori(1, MOD1 // 2) as i:
                for q in range(8):
                    lo(i * 8 + q, q % RAW)
            lo_at(C_IN0)
            dve.wait_ge(mod_col, MOD1)
            dve.wait_ge(xt_cp, KD)

            def add_bias(k0, n):
                b = pc1[:, 32 + k0:32 + k0 + n].unsqueeze(2).to_broadcast([P, n, 2])
                link(V.tensor_tensor(modc[:, k0:k0 + n, :], modc[:, k0:k0 + n, :], b, ALU.add))

            def gain(k0, j, one):
                g = pc2[:, NG + KD * j:NG + KD * (j + 1)].unsqueeze(2).to_broadcast([P, KD, 2])
                m = modc[:, k0:k0 + KD, :]
                if one:
                    link(V.scalar_tensor_tensor(m, m, 1.0, g, ALU.add, ALU.mult))
                else:
                    link(V.tensor_tensor(m, m, g, ALU.mult))

            add_bias(SH_M, 2 * KD)
            gain(SC_M, 0, True)

            def modulate(ks, done, sc, sh, from_psum):
                for k in ks:
                    if from_psum:
                        dve.wait_ge(xt_ps, done + k + 1)
                    src = ps[xt_bank(k, done)[0]] if from_psum else xnT[:, k]
                    V.tensor_scalar(xnT[:, k, 0:CTX], src[:, 0:CTX], modc[:, sc + k, 1:2], modc[:, sh + k, 1:2],
                                    ALU.mult, ALU.add)
                    ins = V.tensor_scalar(xnT[:, k, CTX:T], src[:, CTX:T], modc[:, sc + k, 0:1], modc[:, sh + k, 0:1],
                                          ALU.mult, ALU.add)
                    ins.then_inc(h_f, 1)

            def h_low(ks, done):
                for k in ks:
                    dve.wait_ge(h_hs, done + k + 1)
                    V.tensor_tensor(h_lo[:, k, :], xnT[:, k, :], h_hi[:, k, :].bitcast(F32), ALU.subtract).then_inc(h_ls, 1)

            def mod_and_split(t0, done, sc, sh, from_psum):
                for k in range(KD + 1):
                    if k < KD:
                        modulate([k], done, sc, sh, from_psum)
                    if k:
                        h_low([k - 1], done)
                    if k == 8:
                        lo_at(t0 + 2)
                    if k == 12:
                        lo_at(t0 + 3)

            lo_at(C_IN0 + 1)
            mod_and_split(C_IN0, 0, SC_M, SH_M, False)
            for q in range(4, 8):
                lo_at(C_IN0 + q)

            def element(i, e):
                lcount = [0]

                def llink(ins):
                    lcount[0] += 1
                    ins.then_inc(lch[e], 1)
                    dve.wait_ge(lch[e], i * L_LINKS[e] + lcount[0])

                for q in range(EL):
                    lo_el(i, e, q)
                    if e == 0 and q == 8:
                        dve.wait_ge(l_xp, i + 1)
                        llink(V.tensor_scalar(XC[:, 0:LW], XP[:, 0:LW], pc2[:, at_reg(i + CW)], pc2[:, at_reg(i + CB)],
                                              ALU.mult, ALU.add))
                        for j in range(1, 4):
                            ins = V.scalar_tensor_tensor(XC[:, 0:LW], XP[:, j:j + LW], pc2[:, at_reg(i + (CW + 4 * j))],
                                                         XC[:, 0:LW], ALU.mult, ALU.add)
                            if j < 3:
                                llink(ins)
                        ins.then_inc(l_xc, 1)
                    if e == 1 and q == 5:
                        for d in range(2):
                            dve.wait_ge(l_tanh, i * 4 + (d + 1))
                            sp = sp4[:, at_reg(i + 4 * d)]
                            V.tensor_scalar(RT[d][:, 0:LW], RT[d][:, 0:LW], sp, sp, ALU.mult, ALU.add).then_inc(l_q, 1)
                    if e == 1 and q == 6:
                        for d in range(2):
                            dve.wait_ge(l_tq, i * 2 + (d + 1))
                            llink(V.tensor_scalar(RT[d][:, 0:LW], TT[d][:, 0:LW], 1.0, None, ALU.add))
                            llink(V.reciprocal(RT[d][:, 0:LW], RT[d][:, 0:LW]))
                            V.tensor_tensor(TT[d][:, 0:LW], TT[d][:, 0:LW], RT[d][:, 0:LW], ALU.mult).then_inc(l_s, 1)
                    if e == 1 and q == 8:
                        for d in range(2):
                            dve.wait_ge(l_tanh, i * 4 + (3 + d))
                            llink(V.scalar_tensor_tensor(II[d][:, 0:LW], II[d][:, 0:LW], 1.0, XC[:, 0:LW], ALU.add, ALU.mult))
                    if e == 1 and q == 9:
                        for d in range(2):
                            dve.wait_ge(l_mu, i * 2 + (d + 1))
                            llink(V.scalar_tensor_tensor(II[d][:, 0:LW], TT[d][:, 0:LW], 0.5, II[d][:, 0:LW], ALU.mult, ALU.mult))
                        cx, lt = slice(0, CTX), slice(L0, L0 + LAT)
                        V.tensor_tensor_scan(RT[0][:, cx], AA[0][:, cx], II[0][:, cx], 0.0, ALU.mult, ALU.add)
                        llink(V.tensor_tensor_scan(RT[0][:, lt], AA[0][:, lt], II[0][:, lt], pc2[:, at_reg(i + ST)],
                                                   ALU.mult, ALU.add))
                        cr, lr = slice(CTX - 1, None, -1), slice(L0 + LAT - 1, L0 - 1, -1)
                        V.tensor_tensor_scan(RT[1][:, cr], AA[1][:, cr], II[1][:, cr], 0.0, ALU.mult, ALU.add)
                        llink(V.tensor_tensor_scan(RT[1][:, lr], AA[1][:, lr], II[1][:, lr], pc2[:, at_reg(i + (ST + 4))],
                                                   ALU.mult, ALU.add))
                        V.tensor_copy(stc[:, at_reg(i)], RT[0][:, CTX - 1:CTX])
                        V.tensor_copy(stc[:, at_reg(i + 4)], RT[1][:, 0:1])
                        llink(V.tensor_tensor(II[0][:, 0:LW], RT[0][:, 0:LW], RT[1][:, 0:LW], ALU.add))
                        dve.wait_ge(l_gg, i + 1)
                        V.tensor_tensor(U[:, 0, at_reg(i * P, P)], II[0][:, cx], GG[:, cx], ALU.mult)
                        V.tensor_tensor(U[:, 1:3, at_reg(i * P, P)], II[0][:, lt].rearrange("p (t f) -> p t f", f=P),
                                        GG[:, CTX:T].rearrange("p (t f) -> p t f", f=P), ALU.mult).then_inc(l_y, 1)
                assert lcount[0] == L_LINKS[e]

            for e in range(2):
                element(0, e)
            with dve.Fori(1, N_EL // 2) as i:
                for e in range(2):
                    element(i, e)

            dve.wait_ge(mod_col, MOD_N)
            add_bias(G_M, 4 * KD)
            gain(G_M, 1, False)
            gain(SC_F, 2, True)
            gain(G_F, 3, False)
            for n in range(4):
                dve.wait_ge(mb_hi, n + 1)
                V.tensor_tensor(h_lo[:, 4 + n, :].rearrange("p (t f) -> p t f", f=P), U[:, :, n * P:(n + 1) * P],
                                h_hi[:, 4 + n, :].rearrange("p (t f) -> p t f", f=P).bitcast(F32),
                                ALU.subtract).then_inc(mb_lo, 1)
            dve.wait_ge(lam_ok, 1)

            def row_max(u):
                kind, h, tb = UNITS[u]
                w = width(tb)
                dve.wait_ge(sc_ps, u + 1)
                for j in range(nsoft(kind)):
                    b = ps[2 + 2 * (u % 2) + j]
                    col = 2 * (u % 2) + j
                    scale = 0.125 if kind == "A" else HD ** -0.5
                    src = b[:, 0:w]
                    if kind == "C" and tb > 0:
                        if u >= 2:
                            dve.wait_ge(pt_ps, u - 1)
                        dve.wait_ge(bias_ok, 1)
                        src, scale = prob[u % 2][0][:, 0:w], 1.0
                        V.tensor_scalar(prob[u % 2][0][:, 0:P], b[:, 0:P], HD ** -0.5, None, ALU.mult)
                        link(V.scalar_tensor_tensor(prob[u % 2][0][:, P:w], b[:, P:w], HD ** -0.5,
                                                    nabias[:, h, tb - 1].rearrange("p i w -> p (i w)"), ALU.mult, ALU.add))
                    link(V.tensor_reduce(mxt[:, col:col + 1], src, AX_X, ALU.max))
                    ins = V.tensor_scalar(negm[:, col:col + 1], mxt[:, col:col + 1], -scale, None, ALU.mult)
                ins.then_inc(mx, 1)

            def probabilities(u):
                kind, h, tb = UNITS[u]
                w = width(tb)
                c0 = 2 * (u % 2)
                dve.wait_ge(ex, u + 1)
                pb = prob[u % 2]
                if kind == "A":
                    link(V.reciprocal(prc[:, c0:c0 + 2], psm[:, c0:c0 + 2]))
                    V.tensor_scalar(pb[0][:, 0:w], pb[0][:, 0:w], prc[:, c0:c0 + 1], None, ALU.mult)
                    link(V.tensor_tensor(prc[:, c0 + 1:c0 + 2], prc[:, c0 + 1:c0 + 2], neglam[:, :], ALU.mult))
                    V.scalar_tensor_tensor(pb[0][:, 0:w], pb[1][:, 0:w], prc[:, c0 + 1:c0 + 2], pb[0][:, 0:w],
                                           ALU.mult, ALU.add).then_inc(pr, 1)
                else:
                    link(V.reciprocal(prc[:, c0:c0 + 1], psm[:, c0:c0 + 1]))
                    V.tensor_scalar(pb[0][:, 0:w], pb[0][:, 0:w], prc[:, c0:c0 + 1], None, ALU.mult).then_inc(pr, 1)

            def o_low(u):
                kind, h, tb = UNITS[u]
                if kind == "A":
                    dve.wait_ge(pv_ps, u + 1)
                    V.tensor_copy(U[:, tb, AQ + h * HD:AQ + (h + 1) * HD], ps[7][:, 0:P]).then_inc(oa_cp, 1)
                else:
                    k = KBASE[kind] + h
                    dve.wait_ge(o_hi, u - 11)
                    V.tensor_tensor(h_lo[:, k, tb * P:(tb + 1) * P], ps[7][:, 0:P],
                                    h_hi[:, k, tb * P:(tb + 1) * P].bitcast(F32), ALU.subtract).then_inc(o_fr, 1)

            for s in range(NU + 4):
                if s >= 4:
                    o_low(s - 4)
                if s < NU:
                    row_max(s)
                if 1 <= s < NU + 1:
                    probabilities(s - 1)
                if s == 24:
                    dve.wait_ge(ra_ok, 1)
                    for a in range(12):
                        o = U[:, a % TB, AQ + a // TB * HD:AQ + (a // TB + 1) * HD]
                        V.tensor_scalar(o, o, rsA[:, a:a + 1], 1.0 - LAM_INIT, ALU.mult, ALU.mult).then_inc(oa_sc, 1)
                if s == NU - 1:
                    lo_at(C_OUT)
                    lo_at(C_OUT + 1)
            for h in range(4):
                dve.wait_ge(oa_hi, h + 1)
                V.tensor_tensor(h_lo[:, h, :], ps[h][:, 0:T], h_hi[:, h, :].bitcast(F32), ALU.subtract).then_inc(oa_lo, 1)

            def diagonal(g0, n, cond, idx):
                if idx:
                    dve.wait_ge(g_ps, idx)
                for f in range(4):
                    ins = V.tensor_scalar(diag[:, f, :], ident[:, :], modc[:, g0 + 4 * n + f, cond:cond + 1], None, ALU.mult)
                ins.then_inc(dg_ok, 1)

            def y_gate(y, n, idx):
                dve.wait_ge(g_ps, idx + 2)
                for tb in range(TB):
                    dve.wait_ge(y_cp, 3 * (idx // 2) + tb + 1)
                    V.tensor_tensor(y[:, tb, n * NC:(n + 1) * NC], y[:, tb, n * NC:(n + 1) * NC],
                                    ps[7 if tb == 0 else 6][:, :], ALU.mult).then_inc(y_g, 1)

            def lo_out(t):
                if t not in (C_OUT, C_OUT + 1):
                    lo_at(t)

            for n in range(4):
                lo_out(C_OUT + 4 * n)
                if n:
                    y_gate(y1, n - 1, 2 * (n - 1))
                diagonal(G_M, n, 1, 2 * n)
                for q in (1, 2, 3):
                    lo_out(C_OUT + 4 * n + q)
                diagonal(G_M, n, 0, 2 * n + 1)
            lo_at(C_F1)
            y_gate(y1, 3, 6)
            lo_at(C_F1 + 1)

            def residual(y, rs, loads, done):
                dve.wait_ge(rs_done, rs)
                dve.wait_ge(x1_in, loads)
                for tb in range(TB):
                    V.scalar_tensor_tensor(x_sb[:, tb, :], y[:, tb, :], yrs[:, tb:tb + 1], x_sb[:, tb, :],
                                           ALU.mult, ALU.add).then_inc(done, 1)

            dve.wait_ge(y_g, 12)
            residual(y1, 2, 32, x1_ok)
            rs_count[0] = 3
            dve.wait_ge(x1_ok, 3)
            normed()
            mod_and_split(C_F1, KD, SC_F, SH_F, True)

            def ffn_in(j, first):
                def lo_j(q):
                    lo(j * 8 + (C_F1 + q), (C_F1 + q) % RAW)
                if not first:
                    lo_j(0)
                    dve.wait_ge(w_used, j * 16 + 2 * C_F1)
                    hidden(j - 1)
                    for q in (1, 2, 3):
                        lo_j(q)
                lo_j(4)
                for tb in range(TB):
                    dve.wait_ge(s_tanh, j * 3 + (tb + 1))
                    ins = V.scalar_tensor_tensor(sg[:, tb, :], sg[:, tb, :], 1.0, ps[tb][:, :], ALU.add, ALU.mult)
                ins.then_inc(s_silu, 1)
                for q in (5, 6, 7):
                    lo_j(q)

            def hidden(j):
                dve.wait_ge(s_silu, j + 1)
                dve.wait_ge(ht_ps, j * 4 + 1)
                for tb in range(TB):
                    ins = V.scalar_tensor_tensor(h3[:, tb, :], sg[:, tb, :], 0.5, ps[3 + tb][:, :], ALU.mult, ALU.mult)
                ins.then_inc(h3_ok, 1)

            ffn_in(0, True)
            with dve.Fori(1, FFN_N) as j:
                ffn_in(j, False)

            for n in range(4):
                for q in range(KG2):
                    t = C_F2 + n * KG2 + q
                    lo_at(t)
                    if n == 0 and q == 0:
                        dve.wait_ge(w_used, 2 * C_F2)
                        hidden(FFN_N - 1)
                    dve.wait_ge(jh, t - C_F2 + 1)
                    V.tensor_tensor(j_lo[t % 2][:, :, :], h3T[:, KG * q:KG * q + KG, :], j_hi[t % 2][:, :, :].bitcast(F32),
                                    ALU.subtract).then_inc(jl, 1)
                    if q == 1 and n:
                        y_gate(y2, n - 1, 8 + 2 * (n - 1))
                    if q in (3, 6):
                        diagonal(G_F, n, 1 if q == 3 else 0, 8 + 2 * n + (q == 6))
            y_gate(y2, 3, 14)
            dve.wait_ge(y_g, 24)
            residual(y2, 4, 48, fin)

        @block.gpsimd
        def _(pool):
            G = nc.gpsimd
            count = [0]

            def link(ins):
                count[0] += 1
                ins.then_inc(pch, 1)
                pool.wait_ge(pch, count[0])

            G.memset(ones[:, :], 1.0)
            link(G.memset(negh[:, :], -0.5))

            def inv_rms(out, sums, n, width_):
                link(G.tensor_scalar(out, sums, 1.0 / width_, EPS, ALU.mult, ALU.add))
                return G.tensor_tensor(out, out, negh[:, 0:n], ALU.pow)

            link(G.memset(ppad[:, :, :], 0.0))
            for h in range(4):
                src = bass.AP(tensor=na_rpb.tensor, offset=(h * 15 + 4) * 31, ap=[[0, GRID_W], [31, NA_RHO], [1, 31]])
                pool.dma_start(ppad[:, NA_RHO * h:NA_RHO * (h + 1), 48:79], src).then_inc(rpb_w, 16)
            pool.wait_ge(sq_done, 3)
            inv_rms(xrs[:, :], xss[:, :], 3, D).then_inc(rs_done, 1)
            pool.wait_ge(rpb_w, 64)
            pool.dma_start(rpb_pad, ppad[:, :, :].rearrange("p r w -> p (r w)")).then_inc(rpb_w, 16)
            pool.wait_ge(xn_done, TB)
            G.memset(XP[:, :], 0.0).then_inc(xp_zero, 1)
            pool.dma_start(tables[:, :], tables_d).then_inc(tab_in, 16)
            pool.dma_start(gbc[:, :, :].rearrange("p j d -> p (j d)"),
                           bass.AP(tensor=qk_g.tensor, offset=0, ap=[[0, P], [1, 2 * HD]])).then_inc(tab_in, 16)
            pool.dma_start(lamw[:, :, :].rearrange("p j d -> p (j d)"),
                           bass.AP(tensor=lam_w.tensor, offset=0, ap=[[0, P], [1, 256]])).then_inc(tab_in, 16)
            def halves(v, left):
                n = v.shape[-1]
                while n > left:
                    n //= 2
                    link(G.tensor_tensor(v[:, :, 0:n], v[:, :, 0:n], v[:, :, n:2 * n], ALU.add))

            pool.wait_ge(tab_in, 48)
            lw = lamw[:, :, :].rearrange("p (a b) d -> p a b d", b=2)
            lp = pool_t[:, 0:128].rearrange("p (a d) -> p a d", d=64)
            link(G.tensor_tensor(lp, lw[:, :, 0, :], lw[:, :, 1, :], ALU.mult))
            halves(lp, 2)
            G.tensor_tensor(lamt[:, 0:2], lp[:, :, 0], lp[:, :, 1], ALU.add).then_inc(lam_p, 1)

            def norm_d(heads, col, gi, sl0):
                for tb in range(TB):
                    v = U[:, tb, col:col + heads * HD].rearrange("p (h d) -> p h d", d=HD)
                    sq = pool_t[:, 0:heads * HD].rearrange("p (h d) -> p h d", d=HD)
                    link(G.tensor_tensor(sq, v, v, ALU.mult))
                    s = nds[:, sl0 + tb * heads:sl0 + (tb + 1) * heads]
                    halves(sq, 2)
                    link(G.tensor_tensor(s, sq[:, :, 0], sq[:, :, 1], ALU.add))
                    link(inv_rms(s, s, heads, HD))
                    link(G.tensor_tensor(v, v, s.unsqueeze(2).to_broadcast([P, heads, HD]), ALU.mult))
                    link(G.tensor_tensor(v, v, gbc[:, gi, :].unsqueeze(1).to_broadcast([P, heads, HD]), ALU.mult))

            def rope(col, groups, half, cos0, sin0):
                w = 2 * half
                for tb in (1, 2):
                    for g0 in range(0, groups, 256 // w):
                        ng = min(256 // w, groups - g0)
                        v = U[:, tb, col + g0 * 2 * w:col + (g0 + ng) * 2 * w].rearrange(
                            "p (g a x f) -> p g a x f", a=2, x=2, f=half)
                        x1, x2 = v[:, :, :, 0, :], v[:, :, :, 1, :]
                        tab = lambda c0: tables[:, c0 + (tb - 1) * w:c0 + tb * w].rearrange("p (a f) -> p a f", f=half)\
                            .unsqueeze(1).to_broadcast([P, ng, 2, half])
                        t1, t2, t3 = (pool_t[:, 256 * j:256 * j + ng * w].rearrange("p (g a f) -> p g a f", a=2, f=half)
                                      for j in range(3))
                        G.tensor_tensor(t1, x1, tab(cos0), ALU.mult)
                        G.tensor_tensor(t2, x2, tab(sin0), ALU.mult)
                        link(G.tensor_tensor(t3, x1, tab(sin0), ALU.mult))
                        link(G.tensor_tensor(x1, t1, t2, ALU.subtract))
                        link(G.tensor_tensor(t1, x2, tab(cos0), ALU.mult))
                        link(G.tensor_tensor(x2, t3, t1, ALU.add))

            stores = [0]

            def store(dst, src):
                pool.dma_start(dst, src).then_inc(stored, 16)
                stores[0] += 16

            for n in range(4):
                if n == 0:
                    pool.wait_ge(acc_free, 2)
                else:
                    pool.wait_ge(l_y, n)
                pool.dma_start(gw[:, :, :], gate_w.rearrange("a d g n c e -> (a n) c (d g) e")[n]).then_inc(gw_in, 16)
                G.tensor_copy(AA[0][:, 0:T].rearrange("p (t f) -> p t f", f=P), U[:, :, BX + n * P:BX + (n + 1) * P])
                G.tensor_copy(AA[1][:, 0:T].rearrange("p (t f) -> p t f", f=P), U[:, :, BG + n * P:BG + (n + 1) * P])\
                    .then_inc(l_stage, 1)
                pool.wait_ge(l_xp, n + 1)
                link(G.tensor_tensor(GT[:, 0:T], BGT[:, 0:T], BGT[:, 0:T], ALU.mult))
                link(G.tensor_scalar(GT[:, 0:T], GT[:, 0:T], 0.044715, 1.0, ALU.mult, ALU.add))
                G.tensor_tensor(GT[:, 0:T], GT[:, 0:T], BGT[:, 0:T], ALU.mult).then_inc(l_g1, 1)
                pool.wait_ge(l_g2, n + 1)
                link(G.tensor_scalar(GG[:, 0:T], GG[:, 0:T], 1.0, 0.5, ALU.add, ALU.mult))
                G.tensor_tensor(GG[:, 0:T], GG[:, 0:T], BGT[:, 0:T], ALU.mult).then_inc(l_gg, 1)
                if n == 1:
                    pool.wait_ge(acc_free, 4)
                    rope(AQ, 8, 16, 64, 128)
                    rope(AK, 8, 16, 64, 128)
                    pool.sem_inc(rope_ok, 1)
                if n == 2:
                    pool.wait_ge(acc_free, 5)
                    store(o_diff[0, 0, 0].rearrange("s h d -> s (h d)"), U[:, 0, AK:AK + 512])
                    store(o_diff[0, 0, 1].rearrange("s h d -> s (h d)"), U[:, 0, AV:AV + 512])
            pool.wait_ge(l_y, 4)
            pool.dma_start(kvA[:, :, :], cdiff.rearrange("b a j p h d -> p (b a j) (h d)")).then_inc(kv_in, 16)
            pool.dma_start(kvC[:, :, :], cna.rearrange("b a j p h d -> p (b a j) (h d)")).then_inc(kv_in, 16)
            pool.dma_start(kvD[:, :, :], cgqa.rearrange("b a j p h d -> p (b a j) (h d)")).then_inc(kv_in, 16)
            pool.wait_ge(rpb_w, 80)
            for h in range(4):
                for r in range(4):
                    src = bass.AP(tensor=rpb_pad.tensor, offset=(h * NA_RHO + NA_OFF - r) * PADW + GRID_W - 1,
                                  ap=[[4 * NA_RHO * PADW - 1, GRID_W], [PADW, 4], [1, GRID_W]])
                    pool.dma_start(nabias[r % 2 * GRID_W:(r % 2 + 1) * GRID_W, h, r // 2], src).then_inc(bias_in, 16)
            pool.wait_ge(lam_e, 1)
            link(G.tensor_tensor(lamt[:, 0:1], lamt[:, 3:4], lamt[:, 2:3], ALU.subtract))
            G.tensor_scalar(neglam[:, :], lamt[:, 0:1], 1.0, -LAM_INIT, ALU.mult, ALU.add).then_inc(lam_ok, 1)
            pool.wait_ge(acc_free, 8)
            store(o_na[0, 0, 0].rearrange("s h d -> s (h d)"), U[:, 0, CK:CK + 512])
            store(o_na[0, 0, 1].rearrange("s h d -> s (h d)"), U[:, 0, CV:CV + 512])
            pool.wait_ge(bias_in, 256)
            nb = nabias[:, :, :, :, :].rearrange("p h q i w -> p (h q i) w")
            G.tensor_tensor(nb, nb, tables[:, 0:64].unsqueeze(1).to_broadcast([P, 32, GRID_W]), ALU.add).then_inc(bias_ok, 1)
            pool.wait_ge(acc_free, IN_N)
            norm_d(4, DQ, 0, 0)
            norm_d(2, DK, 1, 12)
            rope(DQ, 6, 32, 192, 320)
            pool.sem_inc(rope_ok, 1)
            store(o_gqa[0, 0, 0].rearrange("s h d -> s (h d)"), U[:, 0, DK:DK + 256])
            store(o_gqa[0, 0, 1].rearrange("s h d -> s (h d)"), U[:, 0, DV:DV + 256])
            pool.wait_ge(st_cp, 1)
            store(o_state.rearrange("b a d (k p) -> (b a d k) p", p=P), rows_st[0:8, :])
            pool.wait_ge(o_fr, 12)
            link(inv_rms(rsA[:, :], ssA[:, :], 12, HD))
            pool.sem_inc(ra_ok, 1)
            pool.wait_ge(pv_ps, NU)
            pool.wait_ge(stored, stores[0])
            pool.dma_start(x_sb[:, 0, :], x_p.rearrange("a s d -> (a s) d")).then_inc(x1_in, 16)
            pool.dma_start(x_sb[:, 1:3, :], x_s.rearrange("a (t p) d -> p (a t) d", p=P)).then_inc(x1_in, 16)

            def y_sums(done):
                pool.wait_ge(acc_free, done)
                ys = yss[:, :].rearrange("p (t n) -> p t n", n=4)
                halves(ys, 2)
                link(G.tensor_tensor(yrs[:, :], ys[:, :, 0], ys[:, :, 1], ALU.add))
                inv_rms(yrs[:, :], yrs[:, :], 3, D).then_inc(rs_done, 1)

            y_sums(IN_N + 4)
            pool.wait_ge(sq_done, 6)
            inv_rms(xrs[:, :], xss[:, :], 3, D).then_inc(rs_done, 1)
            pool.wait_ge(x1_ok, 3)
            pool.wait_ge(xn_done, 6)
            pool.dma_start(x1_dram, x_sb[:, :, :]).then_inc(spill, 16)
            pool.wait_ge(ht_ps, 4 * FFN_N + 1)
            pool.wait_ge(spill, 16)
            pool.dma_start(x_sb[:, :, :], x1_dram).then_inc(x1_in, 16)
            y_sums(IN_N + 8)
            for tb in range(TB):
                pool.wait_ge(fin, tb + 1)
                store(y_p[0] if tb == 0 else y_s[0, (tb - 1) * P:tb * P, :], x_sb[:, tb, :])
            pool.wait_ge(stored, stores[0])


_INS = ["x_prompt", "x_sample", "cache_diff_kv", "state_rglru", "cache_na_kv", "cache_gqa_kv", "c", "c_ctx", "b_mod",
        "norm_g", "diff_lambda_w", "lru_conv_w", "lru_conv_b", "lru_gate_w", "lru_gate_b", "lru_lambda", "na_rpb",
        "gqa_qk_g"]
_OUTS = [(1, CTX, D), (1, LAT, D), (1, 1, 2, CTX, 4, HD), (1, 1, 2, 512), (1, 1, 2, CTX, 4, HD), (1, 1, 2, CTX, 2, HD)]


def weight_tiles(w_mod, w_in, w_out, w_ffn_in, w_ffn_out):
    def tile(w, n, kg):
        block = w[KG * P * kg:KG * P * (kg + 1), NC * n:NC * (n + 1)]
        return block.reshape(KG, P, NC).transpose(1, 0, 2).reshape(P, KG * NC)

    in_n = [3, 4, 0, 1, 2, 5, 6, 7, 8, 9]
    order = [(w_mod, n, kg) for n in range(MOD1) for kg in range(KG)]
    order += [(w_in, in_n[n], kg) for n in range(2) for kg in range(KG)]
    for e in range(N_EL):
        order += [(w_in, in_n[2 + e], kg) if what == "in" else (w_mod, MOD1 + 2 * e + m, kg) for what, m, kg in EL_PLAN]
    order += [(w_out, n, kg) for n in range(D // NC) for kg in range(KG)]
    for j in range(FFN_N):
        order += [(w_ffn_in, n, kg) for n in (FFN_N + j, j) for kg in range(KG)]
    order += [(w_ffn_out, n, kg) for n in range(D // NC) for kg in range(KG2)]
    out = np.empty((len(order), P, KG * NC), w_mod.dtype)
    for t, (w, n, kg) in enumerate(order):
        out[t] = tile(w, n, kg)
    return out


def shape_tables():
    w = np.arange(GRID_W)
    start = np.clip(w - 8, 0, GRID_W - 16)
    inside = (w[None, :] >= start[:, None]) & (w[None, :] < start[:, None] + 16)
    mask = np.where(inside, 0.0, -1e30).astype(np.float32)
    parts = [np.concatenate([mask, mask])]
    t = np.arange(LAT)
    for half in (16, 32):
        m = 2 * half
        freqs = np.float32(10000.0) ** (-np.arange(0, m, 2, dtype=np.float32) / np.float32(m))
        ang = np.stack([(t // GRID_W).astype(np.float32)[:, None] * freqs, (t % GRID_W).astype(np.float32)[:, None] * freqs], 1)
        for f in (np.cos, np.sin):
            v = f(ang.astype(np.float32)).astype(np.float32).reshape(2, P, m)
            parts.append(v.transpose(1, 0, 2).reshape(P, 2 * m))
    return np.ascontiguousarray(np.concatenate(parts, 1))


def kernel(**inputs):
    import concourse.bacc as bacc
    from concourse.bass_utils import run_bass_kernel_spmd

    nc = bacc.Bacc("TRN2", target_bir_lowering=False, num_devices=1)
    inp = {k: np.asarray(v) for k, v in inputs.items()}
    arrays = {"weights": weight_tiles(*(inp[n][0] for n in ("w_mod", "w_in", "w_out", "w_ffn_in", "w_ffn_out")))}
    for name in _INS:
        arrays[name] = np.ascontiguousarray(inp[name])
    arrays["ident_c"] = np.eye(P, dtype=np.float32)
    arrays["tables_c"] = shape_tables()
    aps = [nc.dram_tensor("in_" + n, a.shape, F32, kind="ExternalInput").ap() for n, a in arrays.items()]
    outs = [nc.dram_tensor(f"out_{i}", shape, F32, kind="ExternalOutput").ap() for i, shape in enumerate(_OUTS)]
    build(nc, *aps, *outs)
    r = run_bass_kernel_spmd(nc, [{"in_" + n: a for n, a in arrays.items()}], core_ids=[0])
    return tuple(r.results[0][f"out_{i}"] for i in range(len(_OUTS)))
```
